# Optimizing a Trainium2 kernel written in Bass

```python
import math
import jax, jax.numpy as jnp
from jax import lax
import numpy as np

D_MODEL = 1024
BATCH = 1
SEQ = 256
DEPTH = 4

N_MIXERS = 3
N_A_LAYERS = (DEPTH + 2) // 3
N_B_LAYERS = (DEPTH + 1) // 3
N_C_LAYERS = DEPTH // 3
RMS_EPS = 1e-6

A_EXPAND = 128
A_HEADS = D_MODEL // A_EXPAND
A_HEAD_V = D_MODEL // A_HEADS
A_CHUNK = 64

B_HEAD_DIM = 128
B_HEADS = D_MODEL // B_HEAD_DIM
B_BLOCK = 256
B_TOPK = 3
B_QUERY_BLOCK = 128

REL_BUCKETS = 32
REL_MAX_DISTANCE = 1024

C_WINDOWS = (2, 4, 8, 16)
C_GROUPS = len(C_WINDOWS)
C_GROUP_DIM = D_MODEL // C_GROUPS

D_FF = 4 * D_MODEL

kernel_name = "hybrid_hgrn2_moba_pool_decoder"

def rmsnorm(x, gain):
    xf = x.astype(jnp.float32)
    y = xf * lax.rsqrt(jnp.mean(xf * xf, axis=-1, keepdims=True) + RMS_EPS)
    return (y * gain.astype(jnp.float32)).astype(x.dtype)

def gla_chunkwise(q, k, v, log_f):
    bsz, nh, s, dk = q.shape
    dv = v.shape[-1]
    n = s // A_CHUNK

    def to_chunks(t):
        return t.reshape(bsz, nh, n, A_CHUNK, t.shape[-1]).transpose(2, 0, 1, 3, 4)

    causal = jnp.tril(jnp.ones((A_CHUNK, A_CHUNK), bool))[:, :, None]

    def step(state, xs):
        qc, kc, vc, gc = xs
        b = jnp.cumsum(gc, axis=-2)
        o_inter = jnp.einsum('bhtd,bhde->bhte', qc * jnp.exp(b), state)
        diff = b[:, :, :, None, :] - b[:, :, None, :, :]
        decay = jnp.where(causal, jnp.exp(jnp.where(causal, diff, 0.0)), 0.0)
        attn = jnp.einsum('bhtd,bhsd,bhtsd->bhts', qc, kc, decay)
        o_intra = jnp.einsum('bhts,bhse->bhte', attn, vc)
        b_last = b[:, :, -1:, :]
        new_state = (jnp.exp(b_last[:, :, 0, :, None]) * state
                     + jnp.einsum('bhsd,bhse->bhde', kc * jnp.exp(b_last - b), vc))
        return new_state, o_inter + o_intra

    state0 = jnp.zeros((bsz, nh, dk, dv), jnp.float32)
    _, out = lax.scan(step, state0, (to_chunks(q), to_chunks(k), to_chunks(v), to_chunks(log_f)))
    return out.transpose(1, 2, 0, 3, 4).reshape(bsz, nh, s, dv)

def hgrn2_mixer(h, w_in, lower_bound, head_norm, w_out):
    bsz, s, _ = h.shape
    proj = h @ w_in
    q, f, i, g = jnp.split(proj, 4, axis=-1)

    def heads(t, d):
        return t.reshape(bsz, s, A_HEADS, d).transpose(0, 2, 1, 3).astype(jnp.float32)

    q = jax.nn.silu(heads(q, A_EXPAND))
    f = heads(f, A_EXPAND)
    v = heads(i, A_HEAD_V)
    lb = lower_bound.reshape(1, A_HEADS, 1, A_EXPAND)
    log_f = jnp.logaddexp(jnp.log(lb), jnp.log1p(-lb) + jax.nn.log_sigmoid(f))
    k = (1.0 - lb) * jax.nn.sigmoid(-f)
    o = gla_chunkwise(q, k, v, log_f)
    o = rmsnorm(o, head_norm)
    o = o.transpose(0, 2, 1, 3).reshape(bsz, s, D_MODEL).astype(h.dtype)
    return (o * jax.nn.silu(g)) @ w_out

def t5_bucket(dist):
    n = jnp.maximum(dist, 0)
    max_exact = REL_BUCKETS // 2
    nf = jnp.maximum(n, 1).astype(jnp.float32)
    large = max_exact + (jnp.log(nf / max_exact) / math.log(REL_MAX_DISTANCE / max_exact)
                         * (REL_BUCKETS - max_exact)).astype(jnp.int32)
    large = jnp.minimum(large, REL_BUCKETS - 1)
    return jnp.where(n < max_exact, n, large)

def moba_attention(q, k, v, rel_table):
    bsz, nh, s, dh = q.shape
    n_blk = -(-s // B_BLOCK)
    pad = n_blk * B_BLOCK - s
    kb = jnp.pad(k, ((0, 0), (0, 0), (0, pad), (0, 0))).reshape(bsz, nh, n_blk, B_BLOCK, dh)
    vb = jnp.pad(v, ((0, 0), (0, 0), (0, pad), (0, 0))).reshape(bsz, nh, n_blk, B_BLOCK, dh)
    k_mean = jnp.mean(kb, axis=3)
    gate = jnp.einsum('bhtd,bhnd->bhtn', q, k_mean)
    q_blk = jnp.arange(s) // B_BLOCK
    past = jnp.arange(n_blk)[None, :] < q_blk[:, None]
    gate = jnp.where(past, gate, -jnp.inf)
    n_sel = min(B_TOPK, n_blk)
    _, sel = lax.top_k(gate, n_sel)

    qb = B_QUERY_BLOCK
    n_q = s // qb

    def by_qblock(t):
        return t.reshape(bsz, nh, n_q, qb, t.shape[-1]).transpose(0, 2, 1, 3, 4).reshape(bsz * n_q, nh, qb, t.shape[-1])

    b_ids = jnp.repeat(jnp.arange(bsz), n_q)
    qb_ids = jnp.tile(jnp.arange(n_q), bsz)
    table_hb = rel_table.T.astype(jnp.float32)
    scale = 1.0 / math.sqrt(dh)
    h3 = jnp.arange(nh)[:, None, None]
    h4 = jnp.arange(nh)[:, None, None, None]
    key_off = jnp.arange(B_BLOCK)

    def attend(args):
        qq, sq, b_id, qb_id = args
        kb_b = kb[b_id]
        vb_b = vb[b_id]
        k_sel = kb_b[h3, sq]
        v_sel = vb_b[h3, sq]
        own = (qb_id * qb) // B_BLOCK
        k_own = lax.dynamic_index_in_dim(kb_b, own, axis=1, keepdims=False)
        v_own = lax.dynamic_index_in_dim(vb_b, own, axis=1, keepdims=False)
        t = qb_id * qb + jnp.arange(qb)
        s_sel = jnp.einsum('hqd,hqjkd->hqjk', qq, k_sel) * scale
        dist_sel = t[None, :, None, None] - (sq[..., None] * B_BLOCK + key_off)
        ok_sel = (jnp.arange(n_sel)[None, :, None] < (t // B_BLOCK)[:, None, None])[None]
        s_sel = jnp.where(ok_sel, s_sel + table_hb[h4, t5_bucket(dist_sel)], -jnp.inf)
        s_own = jnp.einsum('hqd,hkd->hqk', qq, k_own) * scale
        dist_own = t[:, None] - (own * B_BLOCK + key_off)[None, :]
        s_own = jnp.where((dist_own >= 0)[None], s_own + table_hb[h3, t5_bucket(dist_own)], -jnp.inf)
        scores = jnp.concatenate([s_sel.reshape(nh, qb, n_sel * B_BLOCK), s_own], axis=-1)
        p = jax.nn.softmax(scores, axis=-1)
        p_sel = p[..., :n_sel * B_BLOCK].reshape(nh, qb, n_sel, B_BLOCK)
        p_own = p[..., n_sel * B_BLOCK:]
        return (jnp.einsum('hqjk,hqjkd->hqd', p_sel, v_sel)
                + jnp.einsum('hqk,hkd->hqd', p_own, v_own))

    out = lax.map(attend, (by_qblock(q), by_qblock(sel), b_ids, qb_ids))
    return out.reshape(bsz, n_q, nh, qb, dh).transpose(0, 2, 1, 3, 4).reshape(bsz, nh, s, dh)

def moba_mixer(h, w_qkv, w_out, rel_table):
    bsz, s, _ = h.shape
    q, k, v = jnp.split(h @ w_qkv, 3, axis=-1)

    def heads(t):
        return t.reshape(bsz, s, B_HEADS, B_HEAD_DIM).transpose(0, 2, 1, 3).astype(jnp.float32)

    o = moba_attention(heads(q), heads(k), heads(v), rel_table)
    o = o.transpose(0, 2, 1, 3).reshape(bsz, s, D_MODEL).astype(h.dtype)
    return o @ w_out

def pool_mixer(h, w_group, scale):
    bsz, s, _ = h.shape
    hg = h.astype(jnp.float32).reshape(bsz, s, C_GROUPS, C_GROUP_DIM)
    cs = jnp.cumsum(hg, axis=1)
    pos1 = jnp.arange(1, s + 1).astype(jnp.float32)
    pooled = []
    for g, w in enumerate(C_WINDOWS):
        cg = cs[:, :, g]
        shifted = jnp.pad(cg, ((0, 0), (w, 0), (0, 0)))[:, :s]
        count = jnp.minimum(pos1, float(w))[None, :, None]
        pooled.append((cg - shifted) / count)
    pooled = jnp.stack(pooled, axis=2)
    mixed = jnp.einsum('bsgc,gcd->bsgd', pooled - hg, w_group.astype(jnp.float32))
    return (mixed.reshape(bsz, s, D_MODEL) * scale.astype(jnp.float32)).astype(h.dtype)

def sqrelu_mlp(h, w1, w2):
    a = jax.nn.relu(h @ w1)
    return (a * a) @ w2

def setup_inputs(seed: int = 0) -> dict:
    key = jax.random.key(seed)
    ks = jax.random.split(key, 16)

    def nrm(k, shape, fan_in):
        return jax.random.normal(k, shape, jnp.float32) * (fan_in ** -0.5)

    def gain(k, shape, s=0.05):
        return 1.0 + s * jax.random.normal(k, shape, jnp.float32)

    return {
        'x': jax.random.normal(ks[0], (BATCH, SEQ, D_MODEL), jnp.float32),
        'norm_mix': gain(ks[1], (DEPTH, D_MODEL)),
        'norm_mlp': gain(ks[2], (DEPTH, D_MODEL)),
        'norm_final': gain(ks[3], (D_MODEL,)),
        'a_w_in': nrm(ks[4], (N_A_LAYERS, D_MODEL, 4 * D_MODEL), D_MODEL),
        'a_lower_bound': jax.random.normal(ks[5], (N_A_LAYERS, A_HEADS * A_EXPAND), jnp.float32),
        'a_head_norm': gain(ks[6], (N_A_LAYERS, A_HEAD_V)),
        'a_w_out': nrm(ks[7], (N_A_LAYERS, D_MODEL, D_MODEL), D_MODEL),
        'b_w_qkv': nrm(ks[8], (N_B_LAYERS, D_MODEL, 3 * D_MODEL), D_MODEL),
        'b_w_out': nrm(ks[9], (N_B_LAYERS, D_MODEL, D_MODEL), D_MODEL),
        'rel_bias': 0.3 * jax.random.normal(ks[10], (REL_BUCKETS, B_HEADS), jnp.float32),
        'c_w_group': nrm(ks[11], (N_C_LAYERS, C_GROUPS, C_GROUP_DIM, C_GROUP_DIM), C_GROUP_DIM),
        'c_scale': gain(ks[12], (N_C_LAYERS, D_MODEL), 0.1),
        'mlp_w1': nrm(ks[13], (DEPTH, D_MODEL, D_FF), D_MODEL),
        'mlp_w2': nrm(ks[14], (DEPTH, D_FF, D_MODEL), D_FF),
    }

def reference(x, norm_mix, norm_mlp, norm_final, a_w_in, a_lower_bound, a_head_norm,
              a_w_out, b_w_qkv, b_w_out, rel_bias, c_w_group, c_scale, mlp_w1, mlp_w2):
    lb_cum = jnp.cumsum(jax.nn.softmax(a_lower_bound.astype(jnp.float32), axis=0), axis=0)
    lower_bounds = lb_cum - lb_cum[0:1]
    for i in range(DEPTH):
        mixer = i % N_MIXERS
        j = i // N_MIXERS
        h = rmsnorm(x, norm_mix[i])
        if mixer == 0:
            y = hgrn2_mixer(h, a_w_in[j], lower_bounds[j], a_head_norm[j], a_w_out[j])
        elif mixer == 1:
            y = moba_mixer(h, b_w_qkv[j], b_w_out[j], rel_bias)
        else:
            y = pool_mixer(h, c_w_group[j], c_scale[j])
        x = x + y.astype(x.dtype)
        x = x + sqrelu_mlp(rmsnorm(x, norm_mlp[i]), mlp_w1[i], mlp_w2[i]).astype(x.dtype)
    return rmsnorm(x, norm_final)


_drawn_inputs = setup_inputs


def setup_inputs(seed=0):
    import zlib

    import numpy as np

    out = dict(_drawn_inputs(seed))
    spreads = {}
    factors = {'a_lower_bound': 3.053}
    for name, (base, spread) in spreads.items():
        noise = np.random.default_rng([zlib.crc32(name.encode()), seed]).standard_normal(out[name].shape)
        drawn = base * np.exp(spread * noise) if base else spread * noise
        out[name] = __import__('jax').numpy.asarray(drawn.astype(out[name].dtype))
    for name, factor in factors.items():
        out[name] = (out[name] * factor).astype(out[name].dtype)
    return out
```

```python
from contextlib import ExitStack

import numpy as np

import concourse.bass as bass
from concourse import mybir

P = 128
ALU = mybir.AluOpType
ACT = mybir.ActivationFunctionType
AX = mybir.AxisListType
F32 = mybir.dt.float32
F32R = mybir.dt.float32r
U8 = mybir.dt.uint8

SEQ, D, DFF, DEPTH, HEADS, BUCKETS = 256, 1024, 4096, 4, 8, 32
KT = D // P
TT = SEQ // P
CH = 512
NCH = DFF // CH
EPS = 1e-6
MASKED = -1e30
LEVELS = [64, 32, 16, 8, 4, 2, 1]
WINDOWS = (2, 4, 8, 16)
BUCKET_FROM = list(range(16)) + [16, 21, 27, 35, 46, 59, 77, 99, 128, 166, 216]
LN_EXP_SET = 6


def decay_sums():
    s, t = np.arange(P)[:, None], np.arange(P)[None, :]
    out = np.zeros((P, 10, P), np.float32)
    for n, m in enumerate(LEVELS):
        mid = t // (2 * m) * (2 * m) + m
        out[:, n] = np.where(t >= mid, (s >= mid) & (s <= t), (s > t) & (s < mid))
    out[:, 7] = s > t
    out[:, 8] = out[:, 6]
    out[:, 9] = s <= t
    return out


def level_masks():
    s, t = np.arange(P)[:, None], np.arange(P)[None, :]
    out = np.zeros((P, 8, P), np.float32)
    for n, m in enumerate(LEVELS):
        out[:, n] = (s // (2 * m) == t // (2 * m)) & (s // m % 2 == 0) & (t // m % 2 == 1)
    out[:, 7] = s == t
    return out


def bucket_rows():
    y = np.arange(2 * SEQ)
    dist = SEQ - 1 - y
    row = np.where(dist < 0, BUCKETS, np.searchsorted(np.array(BUCKET_FROM), np.maximum(dist, 0), side="right") - 1)
    return (np.arange(BUCKETS + 1)[:, None] == row[None, :]).astype(np.float32)


def pool_band():
    out = np.zeros((P, len(WINDOWS), 2, SEQ), np.float32)
    s, t = np.arange(SEQ)[:, None], np.arange(SEQ)[None, :]
    for n, w in enumerate(WINDOWS):
        m = ((s <= t) & (s > t - w)) - np.minimum(t + 1, w) * (s == t)
        out[:, n] = m.reshape(TT, P, SEQ).transpose(1, 0, 2)
    return out


def inverse_counts():
    pos = np.arange(1, SEQ + 1, dtype=np.float32)
    return np.stack([np.float32(1) / np.minimum(pos, np.float32(w)) for w in WINDOWS])


class Chain:

    def __init__(self, eng, sem):
        self.eng, self.own, self.counts, self.last = eng, sem, {}, None

    def did(self, ins, sem=None, value=None):
        key = "own" if sem is None else sem.name
        self.counts[key] = self.counts.get(key, 0) + 1 if value is None else value
        ins.then_inc(self.own if sem is None else sem, 1)
        self.last = (self.own if sem is None else sem, self.counts[key])

    def settle(self):
        if self.last:
            self.eng.wait_ge(*self.last)


def build_decoder(nc, x, norm_mix, norm_mlp, norm_final, a_w_in, a_lower_bound, a_head_norm, a_w_out,
                  b_w_qkv, b_w_out, rel_bias, c_w_group, c_scale, mlp_w1, mlp_w2,
                  c_decay, c_mask, c_bucket, c_inv, c_band, out):
    def cols(w, n):
        return [w[u * 512:(u + 1) * 512, n * CH:(n + 1) * CH].rearrange("(k p) n -> p k n", p=P) for u in range(2)]

    groups = []
    first_group = {}

    def phase(name, sources):
        first_group[name] = len(groups)
        groups.extend(sources)

    for layer in range(DEPTH):
        if layer % 3 == 0:
            j = layer // 3
            order = [2, 3, 0, 1, 4, 5, 6, 7]
            phase(f"in{layer}", [cols(a_w_in[j], n) for n in order])
            phase(f"out{layer}", [cols(a_w_out[j], n) for n in range(2)])
        elif layer % 3 == 1:
            phase(f"in{layer}", [cols(b_w_qkv[0], n) for n in (0, 2, 1, 3, 4, 5)])
            phase(f"out{layer}", [cols(b_w_out[0], n) for n in range(2)])
        else:
            phase(f"in{layer}", [[c_w_group[0, 2 * u:2 * u + 2].rearrange("g (k p) n -> p (g k) n", p=P)
                                  for u in range(2)]])
        phase(f"mlp{layer}", [None] * (2 * NCH))
    n_groups = len(groups)

    first_bank, banks = {}, 0
    for layer in range(DEPTH):
        first_bank[f"in{layer}"] = banks
        banks += {0: 16, 1: 12, 2: 4}[layer % 3]
        first_bank[f"out{layer}"] = banks
        banks += 0 if layer % 3 == 2 else 4
        first_bank[f"mlp{layer}"] = banks
        banks += 2 * NCH

    ctx = ExitStack()
    with ctx:
        def sb(name, shape, dt=F32):
            return ctx.enter_context(nc.sbuf_tensor(name, shape, dt))

        def sem(name):
            return ctx.enter_context(nc.semaphore(name))

        raw = sb("raw", [P, 2, 2, 2048])
        whi = sb("whi", [P, 2, 2, 2048], F32R)
        wlo = sb("wlo", [P, 2, 2, 2048], F32R)
        xT = sb("xT", [P, KT, SEQ])
        hn = sb("hn", [P, KT, SEQ])
        xh = sb("xh", [P, KT, SEQ], F32R)
        xl = sb("xl", [P, KT, SEQ], F32R)
        squares = sb("squares", [P, 2, SEQ])
        rstd = sb("rstd", [P, SEQ])
        ident = sb("ident", [P, P])
        ones = sb("ones", [P, P])
        gains = sb("gains", [P, 82])
        decay = sb("decay", [P, 10, P], F32R)
        masks = sb("masks", [P, 8, P], U8)
        small = sb("small", [P, 16])
        eps_col = sb("eps_col", [P, 1])
        rcol = sb("rcol", [P, TT])
        tab = sb("tab", [BUCKETS + 1, HEADS])
        arena = sb("arena", [P, 13440])
        arena_r = sb("arena_r", [P, 4096], F32R)

        def carve(at, *dims):
            n = int(np.prod(dims))
            v = arena[:, at:at + n]
            names = "abc"[:len(dims)]
            if len(dims) == 1:
                return v
            return v.rearrange(f"p ({' '.join(names)}) -> p {' '.join(names)}", **dict(zip(names[1:], dims[1:])))

        oh = arena_r[:, 0:2048].rearrange("p (a b) -> p a b", a=HEADS)
        ol = arena_r[:, 2048:4096].rearrange("p (a b) -> p a b", a=HEADS)
        scaled = carve(2048, 2, 512)
        act_r = carve(0, 2, 512)
        act_s = carve(1024, 2, 512)
        hh = arena_r[:, 0:2048].rearrange("p (a b c) -> p a b c", a=2, b=4)
        hl = arena_r[:, 2048:4096].rearrange("p (a b c) -> p a b c", a=2, b=4)
        kT = carve(0, HEADS, SEQ)
        qT = carve(2048, HEADS, SEQ)
        v = carve(4096, TT, D)
        Ex = carve(6144, 2, 512)
        Pq = carve(7168, 2, 512)
        Pk = carve(8192, 2, 512)
        att = carve(9216, HEADS, 3 * P)
        C0 = carve(9216, D)
        C1 = carve(10240, D)
        t1 = carve(12288, 512)
        t2 = carve(12800, 512)
        scratch = [(t1, t2), (carve(11264, 512), carve(11776, 512))]
        mask64 = carve(13312, P)
        lfh = arena_r[:, 0:2048].rearrange("p (a b) -> p a b", a=2)
        lfl = arena_r[:, 2048:4096].rearrange("p (a b) -> p a b", a=2)
        decay_in = carve(6144, 10 * P)
        masks_in = carve(7424, 8, P)
        bias = carve(6144, HEADS, SEQ)
        bh = arena_r[:, 0:2048].rearrange("p (a b) -> p a b", a=HEADS)
        bl = arena_r[:, 2048:4096].rearrange("p (a b) -> p a b", a=HEADS)
        probs = carve(8192, 2, 3 * P)
        pT = carve(9216, HEADS, 3 * P)
        flip = sb("flip", [P, P], F32R)
        flip_in = carve(12800, P)
        bias_row = arena[0:HEADS, 12288:12800]
        gain_rows = arena[0:82, 12288:12288 + P]
        bucket = arena[0:BUCKETS + 1, 12800:13312]
        yh, yl = (w.rearrange("p (t a) b -> p t (a b)", t=TT) for w in (oh, ol))
        inv = carve(4096, 4, SEQ)
        x_tok = carve(0, TT, D)
        lb_in = carve(4096, 2, D)
        lb_a = carve(6144, D)

        hb = [ctx.enter_context(nc.psum_tensor(f"hb{i}", [P, 512], F32)) for i in range(2)]
        acc = [ctx.enter_context(nc.psum_tensor(f"acc{i}", [P, 512], F32)) for i in range(4)]
        misc = [ctx.enter_context(nc.psum_tensor(f"misc{i}", [P, 512], F32)) for i in range(2)]

        bias_dram = nc.dram_tensor("bias_rows", [HEADS, 2 * SEQ], F32, kind="Internal").ap()

        raw_in = [[sem(f"raw_in{p}{u}") for u in range(2)] for p in range(2)]
        hi_done, lo_done, down_done = sem("hi_done"), sem("lo_done"), sem("down_done")
        bank_ready, bank_free = sem("bank_ready"), sem("bank_free")
        acc_ready = sem("acc_ready")
        x_ready, sq_ready, sum_ready, ms_mm = sem("x_ready"), sem("sq_ready"), sem("sum_ready"), sem("ms_mm")
        rstd_ready, hn_done = sem("rstd_ready"), sem("hn_done")
        xh_done, xl_done, col_mm, col_ready = sem("xh_done"), sem("xl_done"), sem("col_mm"), sem("col_ready")
        relu_done, scaled_done, s_done, hh_done, hl_done = sem("relu_done"), sem("scaled_done"), sem("s_done"), sem("hh_done"), sem("hl_done")
        act_chain, dve_chain, pool_chain = sem("act_chain"), sem("dve_chain"), sem("pool_chain")
        const_in, lb_loaded, tab_in, inv_in, x_in, decay_loaded = (sem("const_in"), sem("lb_loaded"), sem("tab_in"), sem("inv_in"), sem("x_in"),
                                    sem("decay_loaded"))
        pool_const, gains_T, gains_sb = sem("pool_const"), sem("gains_T"), sem("gains_sb")
        xT_mm = sem("xT_mm")
        decay_ready = sem("decay_ready")
        gate_act, gate_dve = sem("gate_act"), sem("gate_dve")
        k_tok, kT_mm, kT_sb = sem("k_tok"), sem("kT_mm"), sem("kT_sb")
        lf_ready = sem("lf_ready")
        e_mm, ex_done, pq_done, pk_done, g_mm, g_read = (sem("e_mm"), sem("ex_done"), sem("pq_done"),
                                                         sem("pk_done"), sem("g_mm"), sem("g_read"))
        o_mm, osq_done, oms_mm, ors_done, on_done, oh_done, ol_done = (
            sem("o_mm"), sem("osq_done"), sem("oms_mm"), sem("ors_done"), sem("on_done"), sem("oh_done"),
            sem("ol_done"))
        bias_row_mm, bias_row_sb, bias_out, bias_in, bh_done, bl_done = (
            sem("bias_row_mm"), sem("bias_row_sb"), sem("bias_out"), sem("bias_in"), sem("bh_done"), sem("bl_done"))
        s_mm, smax, sexp, sscaled, p_mm, p_sb = (sem("s_mm"), sem("smax"), sem("sexp"), sem("sscaled"),
                                                 sem("p_mm"), sem("p_sb"))
        silu_done = sem("silu_done")
        band_loaded, yh_done, yl_done, pool_mm = sem("band_loaded"), sem("yh_done"), sem("yl_done"), sem("pool_mm")
        out_mm, out_sb, out_dma = sem("out_mm"), sem("out_sb"), sem("out_dma")

        block = ctx.enter_context(nc.Block())

        def w_k(t, g, kt, lo, hi):
            return t[:, g % 2, kt // 4, kt % 4 * CH + lo:kt % 4 * CH + hi]

        def w_b(t, g, kt, f):
            return t[:, g % 2, kt // 2, kt % 2 * D + f * P:kt % 2 * D + (f + 1) * P]

        def mix_norm(layer):
            return 2 * layer

        def gain_col(n, f):
            if n == 2 * DEPTH:
                return 64 + f
            return (0 if n % 2 == 0 else 32) + 8 * (n // 2) + f

        def free_count(layer):
            return {0: 0, 1: 12, 3: 24}[layer]

        def used(g):
            for layer in range(DEPTH):
                for name in ("in", "out", "mlp"):
                    at = first_group.get(f"{name}{layer}")
                    if at is None or g < at:
                        continue
                    k, b = g - at, first_bank[f"{name}{layer}"]
                    if name == "in" and layer % 3 == 2:
                        found = pool_mm, 4, 0
                    elif name != "mlp":
                        found = bank_ready, b + 2 * k + 2, 0
                    elif k == 2 * NCH - 1:
                        found = acc_ready, 4 * (layer + 1), 0
                    elif k > 1 and k % 2 == 0:
                        found = down_done, (NCH - 1) * layer + k // 2, 2
                    else:
                        found = bank_ready, b + 2 * (k if k < 2 else (k + 1) // 2) + 2, 4
            return found

        def o_count(layer):
            return {0: 0, 1: 4, 3: 8}[layer]

        o_banks = [misc[0], misc[1], acc[2], acc[3]]
        ms_banks = [acc[0], acc[1], acc[0], acc[1]]
        o_squares_at = [qT[:, 0:2, :].rearrange("p a b -> p (a b)"), qT[:, 2:4, :].rearrange("p a b -> p (a b)"),
                        Pk[:, 0, :], Pk[:, 1, :]]
        o_at = [kT[:, 0:2, :].rearrange("p a b -> p (a b)"), kT[:, 2:4, :].rearrange("p a b -> p (a b)"),
                Pq[:, 0, :], Pq[:, 1, :]]

        @block.sync
        def _(sp):
            sp.dma_start(x_tok, x[0].rearrange("(t p) d -> p t d", p=P)).then_inc(x_in, 16)
            sp.dma_start(gain_rows[0:32, :], norm_mix.rearrange("l (f p) -> (l f) p", p=P)).then_inc(const_in, 16)
            sp.dma_start(gain_rows[32:64, :], norm_mlp.rearrange("l (f p) -> (l f) p", p=P)).then_inc(const_in, 16)
            sp.dma_start(gain_rows[64:72, :], norm_final.rearrange("(f p) -> f p", p=P)).then_inc(const_in, 16)
            sp.dma_start(gain_rows[72:80, :], c_scale.rearrange("l (f p) -> (l f) p", p=P)).then_inc(const_in, 16)
            sp.dma_start(gain_rows[80:82, :], a_head_norm).then_inc(const_in, 16)

            def load(g, src=None):
                for u in range(2):
                    if g >= 2:
                        sp.wait_ge(lo_done, 2 * (g - 2) + u + 1)
                    s = groups[g][u] if src is None else src[u]
                    n = s.shape[1] * s.shape[2]
                    sp.dma_start(raw[:, g % 2, u, 0:n].rearrange("p (k n) -> p k n", n=s.shape[2]), s)\
                        .then_inc(raw_in[g % 2][u], 16)

            def w1_src(layer, j):
                return cols(mlp_w1[layer], j)

            def w2_src(layer, j):
                return [mlp_w2[layer, j * CH + u * 256:j * CH + (u + 1) * 256, :].rearrange("(k p) n -> p k n", p=P)
                        for u in range(2)]

            for layer in range(DEPTH):
                for g in range(first_group[f"in{layer}"], first_group[f"mlp{layer}"]):
                    load(g)
                    if layer % 3 == 2:
                        sp.dma_start(raw[:, g % 2, :, 1024:2048], c_band.rearrange("p (u w) s t -> p u (w s t)", u=2))\
                            .then_inc(band_loaded, 16)
                    if g == 0:
                        sp.dma_start(masks_in, c_mask).then_inc(decay_loaded, 16)
                        sp.dma_start(decay_in, c_decay.rearrange("p a b -> p (a b)")).then_inc(decay_loaded, 16)
                    if layer == 1 and g == first_group["in1"] + 2:
                        sp.wait_ge(bias_out, 16)
                        sp.dma_start(bias, bass.AP(tensor=bias_dram.tensor, offset=0,
                                                   ap=[[1, P], [2 * SEQ, HEADS], [1, SEQ]])).then_inc(bias_in, 16)
                g0 = first_group[f"mlp{layer}"]
                load(g0, w1_src(layer, 0))
                load(g0 + 1, w1_src(layer, 1))
                load(g0 + 2, w2_src(layer, 0))
                if layer == 2:
                    sp.wait_ge(x_ready, 4 * (2 * layer + 2))
                    sp.dma_start(lb_in, a_lower_bound.rearrange("(a l) d -> a l d", a=1).to_broadcast([P, 2, D]))\
                        .then_inc(lb_loaded, 16)
                with sp.Fori(0, (NCH - 2) // 2) as it:
                    for c in range(4):
                        g = g0 + 3 + c
                        for u in range(2):
                            j = 2 * it + (2 + c // 2 if c % 2 == 0 else 1 + c // 2)
                            if c % 2 == 0:
                                s = mlp_w1[layer, u * 512:(u + 1) * 512, bass.ds(j * CH, CH)]
                            else:
                                s = mlp_w2[layer, bass.ds(j * CH + u * 256, 256), :]
                            s = s.rearrange("(k p) n -> p k n", p=P)
                            sp.wait_ge(lo_done, 8 * it + (2 * (g - 2) + u + 1))
                            sp.dma_start(raw[:, g % 2, u, :].rearrange("p (k n) -> p k n", n=s.shape[2]), s)\
                                .then_inc(raw_in[g % 2][u], 16)
                load(g0 + 2 * NCH - 1, w2_src(layer, NCH - 1))
                if layer == 0:
                    sp.wait_ge(hl_done, 2 * NCH)
                    sp.dma_start(bucket, c_bucket).then_inc(tab_in, 16)
                    sp.dma_start(tab[0:BUCKETS, :], rel_bias).then_inc(tab_in, 16)
                if layer == 1:
                    sp.wait_ge(hl_done, 2 * NCH * 2)
                    sp.dma_start(inv, c_inv.rearrange("(a g) t -> a g t", a=1).to_broadcast([P, 4, SEQ]))\
                        .then_inc(inv_in, 16)
            for t in range(TT):
                sp.wait_ge(out_sb, 2 * (t + 1))
                sp.dma_start(out[0, t * P:(t + 1) * P, :], x_tok[:, t, :]).then_inc(out_dma, 16)
            sp.wait_ge(out_dma, 16 * TT)

        @block.tensor
        def _(pe):
            def ones_mm(n):
                pe.wait_ge(sum_ready, n + 1)
                if n:
                    pe.wait_ge(rstd_ready, n)
                for i in range(2):
                    mm = pe.matmul(misc[0][:, 0:SEQ], ones[:, :], squares[:, i, :], start=i == 0, stop=i == 1)
                mm.then_inc(ms_mm, 1)

            def token_column(n):
                pe.wait_ge(rstd_ready, n + 1)
                if n == mix_norm(1):
                    pe.wait_ge(bias_row_sb, 1)
                for t in range(TT):
                    mm = pe.transpose(misc[1][:, t * P:(t + 1) * P], rstd[:, t * P:(t + 1) * P], ident[:, :])
                mm.then_inc(col_mm, 1)

            def norm_steps(n, then=lambda: None):
                at = [0]

                def step():
                    at[0] += 1
                    if at[0] == 2:
                        ones_mm(n)
                    if at[0] == 3:
                        token_column(n)
                    then()
                return step

            seen = set()

            def need_weights(g, u):
                pe.wait_ge(lo_done, 2 * g + u + 1)

            def need_x(n, f):
                if (n, f) not in seen:
                    seen.add((n, f))
                    pe.wait_ge(xl_done, 8 * n + f + 1)

            def x_banks(n):
                def wait(k):
                    if k >= 2:
                        pe.wait_ge(x_ready, 4 * n + k - 1)
                return wait

            def mixer_banks(layer, first=0):
                def wait(k):
                    if k >= first + 2:
                        pe.wait_ge(bank_free, free_count(layer) + k - first - 1)
                return wait

            def t_block(g, bank, half, fcol, need, k0=0, k1=KT, x_=(xh, xl)):
                o = bank[:, half * SEQ:(half + 1) * SEQ]
                for kt in range(k0, k1):
                    need(kt)
                    if kt % 4 == 0:
                        need_weights(g, kt // 4)
                    h, l = (w_k(t, g, kt, fcol * P, (fcol + 1) * P) for t in (whi, wlo))
                    pe.matmul(o, h, x_[0][:, kt, :], start=kt == 0 and half == 0, stop=False,
                              skip_group_check=True)
                    pe.matmul(o, h, x_[1][:, kt, :], start=False, stop=False, skip_group_check=True)
                    mm = pe.matmul(o, l, x_[0][:, kt, :], start=False, stop=kt == KT - 1,
                                   skip_group_check=True)
                return mm

            def w_half(g, bank, t, k0, k1, need):
                for kt in range(k0, k1):
                    need(kt)
                    if kt % 4 == 0:
                        need_weights(g, kt // 4)
                    h, l = (w_k(x_, g, kt, 0, CH) for x_ in (whi, wlo))
                    xs, ls = xh[:, kt, t * P:(t + 1) * P], xl[:, kt, t * P:(t + 1) * P]
                    pe.matmul(bank[:, :], xs, h, start=kt == 0, stop=False)
                    pe.matmul(bank[:, :], xs, l, start=False, stop=False)
                    mm = pe.matmul(bank[:, :], ls, h, start=False, stop=kt == KT - 1)
                return mm

            def group(kind, g, k, last_read, need, between=lambda: None, banks=hb, x_=(xh, xl),
                      early=False):
                for i in range(2):
                    last_read(k + i)
                    if early and i == 0:
                        for q in range(2):
                            t_block(g, banks[i], q, 2 * i + q, need, 0, 6, x_)
                    for q in range(2):
                        if kind == "T":
                            mm = t_block(g, banks[i], q, 2 * i + q, need, 6 if early and i == 0 else 0, KT, x_)
                        else:
                            mm = w_half(g, banks[i], i, 4 * q, 4 * q + 4, need)
                        if q:
                            mm.then_inc(bank_ready, 1)
                        between()

            def mlp_up(layer, g, lo_at, r_at=None):
                def tiles(i, q, k0, k1):
                    o = hb[i][:, q * SEQ:(q + 1) * SEQ]
                    for kt in range(k0, k1):
                        need_x(2 * layer + 1, kt)
                        if i == 0 and q == 0 and kt % 4 == 0:
                            pe.wait_ge(lo_done, lo_at + (kt // 4 + 1))
                        h, l = (w_k(t, g, kt, (2 * i + q) * P, (2 * i + q + 1) * P) for t in (whi, wlo))
                        pe.matmul(o, h, xh[:, kt, :], start=kt == 0 and q == 0, stop=False, skip_group_check=True)
                        pe.matmul(o, h, xl[:, kt, :], start=False, stop=False, skip_group_check=True)
                        mm = pe.matmul(o, l, xh[:, kt, :], start=False, stop=kt == KT - 1, skip_group_check=True)
                    return mm

                for i in range(2):
                    if r_at is not None:
                        pe.wait_ge(relu_done, r_at + (i - 1))
                    else:
                        pe.wait_ge(x_ready, 4 * (2 * layer + 1) + 3 + i)
                    k0 = 0
                    if r_at is None and i == 0:
                        k0 = 6
                        for q in range(2):
                            tiles(i, q, 0, k0)
                    for q in range(2):
                        mm = tiles(i, q, k0, KT)
                    mm.then_inc(bank_ready, 1)

            def mlp_down(layer, g, par, lo_at, hl_at, first=False, last=False):
                for f in range(KT):
                    o = acc[f // 2][:, f % 2 * SEQ:(f % 2 + 1) * SEQ]
                    for kt in range(4):
                        if f == 0 and kt % 2 == 0:
                            pe.wait_ge(lo_done, lo_at + (kt // 2 + 1))
                            pe.wait_ge(hl_done, hl_at + (kt // 2 + 1))
                        h, l = (w_b(t, g, kt, f) for t in (whi, wlo))
                        st = first and kt == 0 and f % 2 == 0
                        pe.matmul(o, h, hh[:, par, kt, :], start=st, stop=False, skip_group_check=True)
                        pe.matmul(o, h, hl[:, par, kt, :], start=False, stop=False, skip_group_check=True)
                        mm = pe.matmul(o, l, hh[:, par, kt, :], start=False, stop=last and kt == 3,
                                       skip_group_check=True)
                    if last and f % 2:
                        mm.then_inc(acc_ready, 1)
                    if not last and f == KT - 1:
                        mm.then_inc(down_done, 1)

            pe.wait_ge(pool_const, 2)
            pe.wait_ge(const_in, 16 * 5)
            pe.transpose(misc[1][:, 0:82], gain_rows, ident[0:82, 0:82]).then_inc(gains_T, 1)
            pe.wait_ge(x_in, 16)
            for f in range(KT):
                for t in range(TT):
                    mm = pe.transpose(acc[f // 2][:, (f % 2 * TT + t) * P:(f % 2 * TT + t + 1) * P],
                                      x_tok[:, t, f * P:(f + 1) * P], ident[:, :])
                if f % 2:
                    mm.then_inc(xT_mm, 1)

            def outputs(weights, p):
                for i in range(2):
                    h = 2 * p + i
                    vt = [v[:, t, h * P:(h + 1) * P] for t in range(TT)]
                    o = o_banks[p][:, i * SEQ:(i + 1) * SEQ]
                    pe.matmul(o[:, 0:P], vt[0], weights[:, h, 0:P], start=True, stop=True)
                    pe.matmul(o[:, P:SEQ], vt[0], weights[:, h, P:SEQ], start=True, stop=False)
                    mm = pe.matmul(o[:, P:SEQ], vt[1], weights[:, h, SEQ:SEQ + P], start=False, stop=True)
                mm.then_inc(o_mm, 1)

            for layer in range(DEPTH):
                n = mix_norm(layer)
                g0, b0 = first_group[f"in{layer}"], first_bank[f"in{layer}"]
                need = lambda kt, n=n: need_x(n, kt)
                j = layer // 3
                if layer % 3 == 0:
                    free = mixer_banks(layer, 4)
                    def acc_read(k):
                        pe.wait_ge(x_ready, 4 * n + k + 1)

                    group("W", g0, 0, acc_read, need, norm_steps(n), acc[0:2])
                    group("W", g0 + 1, 2, lambda k: None, need, banks=acc[2:4])

                    def k_transposes(c):
                        pe.wait_ge(k_tok, 4 * j + 2 * (c // 2) + 2)
                        if c < 2:
                            pe.wait_ge(col_ready, n // 2 + 1)
                        if c >= 2:
                            pe.wait_ge(kT_sb, 4 * j + c - 1)
                        for h in range(2):
                            for t in range(TT):
                                mm = pe.transpose(misc[c % 2][:, (h * TT + t) * P:(h * TT + t + 1) * P],
                                                  v[:, t, (2 * c + h) * P:(2 * c + h + 1) * P], ident[:, :])
                        mm.then_inc(kT_mm, 1)

                    for c in range(2):
                        group("T", g0 + 2 + c, 4 + 2 * c, free, need)
                        k_transposes(2 * c)
                        k_transposes(2 * c + 1)

                    def e_step(i):
                        h, c = divmod(i, 4)
                        e = acc[i % 2]
                        base = 32 * j
                        if i == 0:
                            pe.wait_ge(lf_ready, 4 * (j + 1))
                            pe.wait_ge(decay_ready, 1)
                        if i >= 2:
                            pe.wait_ge(ex_done, base + i - 1)
                        for t in range(TT):
                            o = e[:, t * 256:(t + 1) * 256]
                            slot = 8 if (c == 3 and t == 1) else 2 * c
                            r = decay[:, slot:slot + 2, :]
                            pe.matmul(o, lfh[:, t, h * P:(h + 1) * P], r, start=True, stop=False)
                            mm = pe.matmul(o, lfl[:, t, h * P:(h + 1) * P], r, start=False, stop=True)
                        mm.then_inc(e_mm, 1)

                    def g_step(i):
                        h, c = divmod(i, 5)
                        gb = acc[2 + i % 2]
                        if i >= 2:
                            pe.wait_ge(g_read, 40 * j + i - 1)
                        if c < 4:
                            pe.wait_ge(pq_done, 32 * j + 4 * h + c + 1)
                            pe.wait_ge(pk_done, 32 * j + 4 * h + c + 1)
                            p = (4 * h + c) % 2
                            for q in range(4 if c < 3 else 3):
                                lev, t = divmod(q, 2)
                                tk = 0 if (c == 3 and lev == 1) else t
                                tq = 1 if (c == 3 and lev == 1) else t
                                at = lambda tile: slice(tile * 256 + lev * P, tile * 256 + (lev + 1) * P)
                                mm = pe.matmul(gb[:, q * P:(q + 1) * P], Pk[:, p, at(tk)], Pq[:, p, at(tq)],
                                               start=True, stop=True)
                        else:
                            for t in range(TT):
                                s = slice(t * P, (t + 1) * P)
                                mm = pe.matmul(gb[:, s], kT[:, h, s], qT[:, h, s], start=True, stop=True)
                        mm.then_inc(g_mm, 1)

                    todo = []
                    ei = 0
                    for i in range(40):
                        h, c = divmod(i, 5)
                        while ei < min(32, 4 * h + min(c, 3) + 3):
                            todo.append(("e", ei))
                            ei += 1
                        todo.append(("g", i))
                    quarter = [-1]

                    def some_steps():
                        if quarter[0] < 0:
                            quarter[0] = 0
                            return
                        if quarter[0] == 0:
                            pe.wait_ge(kT_sb, 4 * (j + 1))
                            pe.wait_ge(silu_done, 8 * j + 4)
                        per = 5 if quarter[0] % 2 == 0 else 4
                        quarter[0] += 1
                        for kind, i in todo[:per]:
                            (e_step if kind == "e" else g_step)(i)
                        del todo[:per]

                    for c, kind in enumerate("WWTT"):
                        group(kind, g0 + 4 + c, 8 + 2 * c, free, need, some_steps)

                    def oms_step(p):
                        pe.wait_ge(osq_done, 4 * j + p + 1)
                        if p >= 2:
                            pe.wait_ge(ors_done, 4 * j + p - 1)
                        pe.matmul(ms_banks[p][:, :], ones[:, :], o_squares_at[p], start=True, stop=True)\
                            .then_inc(oms_mm, 1)

                    pe.wait_ge(g_read, 40 * j + 20)
                    pe.wait_ge(bank_free, free_count(layer) + 8)
                    outputs(att, 0)
                    outputs(att, 1)
                    while todo:
                        some_steps()
                    pe.wait_ge(ex_done, 32 * (j + 1))
                    oms_step(0)
                    oms_step(1)
                    pe.wait_ge(g_read, 40 * (j + 1))
                    for p in (2, 3):
                        outputs(att, p)
                    for p in (2, 3):
                        oms_step(p)
                    pe.wait_ge(bank_free, free_count(layer) + 12)
                elif layer % 3 == 1:
                    pe.wait_ge(tab_in, 32)
                    pe.wait_ge(pool_const, 5)
                    pe.matmul(misc[1][0:HEADS, :], tab[:, :], bucket, start=True, stop=True).then_inc(bias_row_mm, 1)
                    def s_step(h):
                        s = acc[h % 2]
                        pe.wait_ge(bank_free, free_count(layer) + 4 * (h // 4 + 1))
                        if h == 0:
                            pe.wait_ge(bl_done, 1)
                        if h >= 2:
                            pe.wait_ge(sexp, 2 * (h - 1))
                        for t, o, ks in ((0, slice(0, P), slice(P, SEQ)), (1, slice(P, P + SEQ), slice(0, SEQ))):
                            pe.matmul(s[:, o], flip[:, :], bh[:, h, ks], start=True, stop=False)
                            pe.matmul(s[:, o], flip[:, :], bl[:, h, ks], start=False, stop=False)
                            mm = pe.matmul(s[:, o], qT[:, h, t * P:(t + 1) * P], kT[:, h, 0:(t + 1) * P],
                                           start=False, stop=True)
                        mm.then_inc(s_mm, 1)

                    def p_step(h):
                        pe.wait_ge(sscaled, 2 * (h + 1))
                        if h >= 2:
                            pe.wait_ge(p_sb, h - 1)
                        for q in range(3):
                            mm = pe.transpose(acc[2 + h % 2][:, q * P:(q + 1) * P], probs[:, h % 2, q * P:(q + 1) * P],
                                              ident[:, :])
                        mm.then_inc(p_mm, 1)

                    quarter = [0]

                    def some_steps():
                        h, odd = divmod(quarter[0], 2)
                        if not odd and 0 <= h - 4 < HEADS:
                            s_step(h - 4)
                        if odd and 0 <= h - 5 < HEADS:
                            p_step(h - 5)
                        quarter[0] += 1

                    for c in range(6):
                        group("TTTTWW"[c], g0 + c, 2 * c, mixer_banks(layer), need,
                              some_steps if c else norm_steps(n, some_steps), early=c == 0)
                    while quarter[0] < 2 * (HEADS + 5):
                        some_steps()
                    pe.wait_ge(p_sb, HEADS)
                    pe.wait_ge(bank_free, free_count(layer) + 12)
                    for h2 in range(4):
                        outputs(pT, h2)
                if layer % 3 != 2:
                    go, bo = first_group[f"out{layer}"], first_bank[f"out{layer}"]
                    need_o = lambda kt, layer=layer: pe.wait_ge(ol_done, o_count(layer) + kt // 2 + 1)
                    state = {"asked": 0}

                    def need_o_once(kt):
                        if state["asked"] <= kt:
                            state["asked"] = kt + 1
                            need_o(kt)

                    for c in range(2):
                        group("T", go + c, 2 * c, x_banks(n + 1), need_o_once, x_=(oh, ol))
                else:
                    for c in range(2):
                        for t in range(TT):
                            if c == 0:
                                pe.wait_ge(x_ready, 4 * n + t + 1)
                            for i in range(2):
                                o = acc[2 * c + t][:, i * SEQ:(i + 1) * SEQ]
                                need_weights(g0, c)
                                for kt in range(2):
                                    f = 2 * (2 * c + i) + kt
                                    need(f)
                                    at = (2 * i + kt) * SEQ
                                    h, l = (w[:, g0 % 2, c, at:at + SEQ] for w in (whi, wlo))
                                    xs, ls = (x_[:, f, t * P:(t + 1) * P] for x_ in (xh, xl))
                                    pe.matmul(o, xs, h, start=kt == 0, stop=False)
                                    pe.matmul(o, xs, l, start=False, stop=False)
                                    mm = pe.matmul(o, ls, h, start=False, stop=kt == 1)
                            mm.then_inc(bank_ready, 1)
                    ones_mm(n)
                    token_column(n)
                    for k in range(4):
                        x_banks(n + 1)(k)
                        pe.wait_ge(yl_done, 2 * (k // 2) + 2)
                        for i in range(2):
                            f = 2 * k + i
                            o = hb[k % 2][:, i * SEQ:(i + 1) * SEQ]
                            for t in range(TT):
                                for y in (yh, yl):
                                    at = 1024 + k % 2 * 512 + t * SEQ
                                    mm = pe.matmul(o, y[:, t, f * P:(f + 1) * P],
                                                   whi[:, g0 % 2, k // 2, at:at + SEQ],
                                                   start=t == 0 and y is yh, stop=t == 1 and y is yl)
                        mm.then_inc(pool_mm, 1)
                g, b = first_group[f"mlp{layer}"], first_bank[f"mlp{layer}"]
                hl0 = 2 * NCH * layer
                mlp_up(layer, g, 2 * g)
                ones_mm(n + 1)
                mlp_up(layer, g + 1, 2 * (g + 1), hl0 + 2)
                mlp_down(layer, g + 2, 0, 2 * (g + 2), hl0, first=True)
                with pe.Fori(0, (NCH - 2) // 2) as it:
                    for c in range(2):
                        mlp_up(layer, g + 3 + 2 * c, 8 * it + 2 * (g + 3 + 2 * c), 4 * it + (hl0 + 4 + 2 * c))
                        mlp_down(layer, g + 4 + 2 * c, (1 + c) % 2, 8 * it + 2 * (g + 4 + 2 * c),
                                 4 * it + (hl0 + 2 * (1 + c)))

                mlp_down(layer, g + 2 * NCH - 1, 1, 2 * (g + 2 * NCH - 1), hl0 + 2 * NCH - 2, last=True)

            n = 2 * DEPTH
            for f in range(KT):
                pe.wait_ge(sq_ready, 2 * n + f // 4 + 1)
                if f == 0:
                    pe.wait_ge(rstd_ready, n)
                mm = pe.matmul(misc[0][:, 0:SEQ], ones[:, :], hn[:, f, :], start=f == 0, stop=f == KT - 1)
            mm.then_inc(ms_mm, 1)

            for t in range(TT):
                for c in range(2):
                    for f in range(4 * c, 4 * c + 4):
                        pe.wait_ge(hn_done, f + 1)
                        mm = pe.transpose(acc[2 * t + c][:, f % 4 * P:(f % 4 + 1) * P],
                                          hn[:, f, t * P:(t + 1) * P], ident[:, :])
                    mm.then_inc(out_mm, 1)

        @block.scalar
        def _(act):
            ch = Chain(act, act_chain)
            act.add_instruction(mybir.InstLoadActFuncSet(name=nc.get_next_instruction_name(), engine=act.engine,
                                                         act_func_set_id=LN_EXP_SET, ins=[], outs=[]))

            def split_unit(g, u, it=None, n=2048):
                loads = 16 * (g // 2 + 1)
                act.wait_ge(raw_in[g % 2][u], loads if it is None else 32 * it + loads)
                if g >= 2:
                    signal, at, step = used(g - 2)
                    act.wait_ge(signal, at if it is None else step * it + at)
                act.activation(whi[:, g % 2, u, 0:n], raw[:, g % 2, u, 0:n], ACT.Copy).then_inc(hi_done, 1)

            def split(g, it=None, n=2048):
                for u in range(2):
                    split_unit(g, u, it, n)

            def take_x(n, between={}):
                for f in range(KT):
                    act.wait_ge(x_ready, 4 * n + f // 2 + 1)
                    if n < 2 * DEPTH:
                        if f == 0 and n == 0:
                            act.wait_ge(gains_sb, 1)
                        act.activation(xh[:, f, :], xT[:, f, :], ACT.Copy, scale=gains[:, gain_col(n, f):gain_col(n, f) + 1])\
                            .then_inc(xh_done, 1)
                    if f in between:
                        between[f]()
                    if f % 4 == 3:
                        fs = slice(f - 3, f + 1)
                        act.activation(hn[:, fs, :], xT[:, fs, :], ACT.Square).then_inc(sq_ready, 1)

            def rms(n):
                act.wait_ge(ms_mm, n + 1)
                if n == 0:
                    act.wait_ge(pool_const, 3)
                ch.did(act.activation(rstd[:, :], misc[0][:, 0:SEQ], ACT.Ln, scale=1.0 / D, bias=eps_col[:, :]))
                ch.settle()
                act.activation(rstd[:, :], rstd[:, :], ACT.Exp, scale=-0.5).then_inc(rstd_ready, 1)

            take_x(0, {3: lambda: split_unit(0, 0), 5: lambda: split_unit(0, 1)})
            act.wait_ge(decay_loaded, 32)
            act.activation(decay[:, :, :], decay_in.rearrange("p (a b) -> p a b", b=P), ACT.Copy)\
                .then_inc(decay_ready, 1)

            turns = {"act": 0, "dve": 0}

            def turn(ins):
                ins.then_inc(gate_act, 1)
                turns["act"] += 1

            def after_dve():
                turns["dve"] += 1
                act.wait_ge(gate_dve, turns["dve"])

            def ln_1p_exp(src, dst):
                ch.did(act.activation(dst, src, ACT.Abs))
                ch.settle()
                ch.did(act.activation(dst, dst, ACT.Exp, scale=-1.0))
                ch.settle()
                turn(act.activation(dst, dst, ACT.Ln, bias=1.0))

            for layer in range(DEPTH):
                n = mix_norm(layer)
                g0, b0 = first_group[f"in{layer}"], first_bank[f"in{layer}"]
                j = layer // 3
                split(g0 + 1)
                rms(n)
                if layer == 3:
                    after_dve()
                if layer % 3 == 0:
                    def gate_a(c, t):
                        z = v[:, t, c * CH:(c + 1) * CH]
                        act.wait_ge(col_ready, n // 2 + 1)
                        act.wait_ge(bank_ready, b0 + 2 * c + t + 1)
                        ch.did(act.activation(z, acc[2 * c + t][:, :], ACT.Copy, scale=rcol[:, t:t + 1]))
                        ch.settle()
                        ln_1p_exp(z, scratch[t][0])

                    def gate_b(c, t):
                        if layer == 3:
                            after_dve()
                            ln_1p_exp(scratch[t][0], scratch[t][0])

                    def gate_c(c, t):
                        cs = slice(c * CH, (c + 1) * CH)
                        after_dve()
                        turn(act.activation(lfh[:, t, cs], scratch[t][1], ACT.Copy))
                        act.activation(v[:, t, cs], v[:, t, cs], ACT.Exp).then_inc(k_tok, 1)

                    def silu_a(k, s, z):
                        act.wait_ge(bank_free, free_count(layer) + k - 3)
                        done = k - 6 if k < 8 else k - 8
                        if 8 * j + done > 0:
                            act.wait_ge(silu_done, 8 * j + done)
                        ln_1p_exp(z.rearrange("p a b -> p (a b)"), scratch[s][0])

                    def silu_b(s):
                        after_dve()
                        turn(act.activation(scratch[s][0], scratch[s][1], ACT.Exp))

                    def kT_copy(k):
                        act.wait_ge(kT_mm, 4 * j + k + 1)
                        act.activation(kT[:, 2 * k:2 * k + 2, :],
                                       misc[k % 2][:, :].rearrange("p (a b) -> p a b", a=2), ACT.Copy)\
                            .then_inc(kT_sb, 1)

                    for c in range(2):
                        gate_a(c, 0)
                        split_unit(g0 + 2 + c, 0)
                        if c:
                            split_unit(g0 + 3, 1)
                        gate_a(c, 1)
                        if not c:
                            split_unit(g0 + 2, 1)
                        gate_b(c, 0)
                        gate_b(c, 1)
                        gate_c(c, 0)
                        gate_c(c, 1)
                    def q_bank(k):
                        return qT[:, 2 * (k - 4):2 * (k - 4) + 2, :]

                    silu_a(4, 0, q_bank(4))
                    silu_a(5, 1, q_bank(5))
                    kT_copy(0)
                    kT_copy(1)
                    split_unit(g0 + 4, 0)
                    silu_b(0)
                    silu_b(1)
                    split_unit(g0 + 4, 1)
                    silu_a(6, 0, q_bank(6))
                    silu_a(7, 1, q_bank(7))
                    kT_copy(2)
                    kT_copy(3)
                    silu_b(0)
                    silu_b(1)

                    def ex_step(i):
                        act.wait_ge(e_mm, 32 * j + i + 1)
                        if i >= 2:
                            act.wait_ge(pq_done, 32 * j + i - 1)
                            act.wait_ge(pk_done, 32 * j + i - 1)
                        act.activation(Ex[:, i % 2, :], acc[i % 2][:, :], ACT.Exp).then_inc(ex_done, 1)

                    for k in range(8):
                        ex_step(4 * k)
                        split_unit(g0 + 5 + k // 2, k % 2)
                        if k > 4:
                            silu_a(7 + k, 0, hn[:, 2 * (k - 5):2 * (k - 5) + 2, :])
                        ex_step(4 * k + 1)
                        ex_step(4 * k + 2)
                        if k > 4:
                            silu_b(0)
                        ex_step(4 * k + 3)
                    def o_squares(p):
                        act.wait_ge(o_mm, o_count(layer) + p + 1)
                        if p >= 2:
                            act.wait_ge(g_mm, 40 * (j + 1))
                        act.activation(o_squares_at[p], o_banks[p][:, :], ACT.Square).then_inc(osq_done, 1)

                    def o_rstd(p):
                        act.wait_ge(oms_mm, 4 * j + p + 1)
                        act.wait_ge(pq_done, 32 * (j + 1))
                        act.wait_ge(pk_done, 32 * (j + 1))
                        if p >= 2:
                            act.wait_ge(on_done, 4 * j + p - 1)
                        r = Ex[:, p % 2, :]
                        ch.did(act.activation(r, ms_banks[p][:, :], ACT.Ln, scale=1.0 / P, bias=eps_col[:, :]))
                        ch.settle()
                        act.activation(r, r, ACT.Exp, scale=-0.5).then_inc(ors_done, 1)

                    def o_hi(p):
                        act.wait_ge(on_done, 4 * j + p + 1)
                        act.activation(oh[:, 2 * p:2 * p + 2, :], o_at[p].rearrange("p (a b) -> p a b", a=2),
                                       ACT.Copy).then_inc(oh_done, 1)

                    o_squares(0)
                    o_squares(1)
                    silu_a(15, 0, hn[:, 6:8, :])
                    o_rstd(0)
                    silu_b(0)
                    o_rstd(1)
                    o_hi(0)
                    o_squares(2)
                    o_hi(1)
                    o_squares(3)
                    o_rstd(2)
                    o_rstd(3)
                    o_hi(2)
                    o_hi(3)
                    split(first_group[f"out{layer}"] + 1)
                elif layer % 3 == 1:
                    def softmax(h):
                        act.wait_ge(smax, h + 1)
                        if h >= 2:
                            act.wait_ge(p_mm, h - 1)
                        for t, cs in ((0, slice(0, P)), (1, slice(P, 3 * P))):
                            k = 2 * (h % 2) + t
                            ins = act.activation(probs[:, h % 2, cs], acc[h % 2][:, cs], ACT.Exp,
                                                 bias=small[:, 4 + k:5 + k], accum_out=small[:, 8 + k:9 + k])
                            ins.then_inc(sexp, 1)

                    def pt_copy(h):
                        act.wait_ge(p_mm, h + 1)
                        act.activation(pT[:, h, :], acc[2 + h % 2][:, 0:3 * P], ACT.Copy).then_inc(p_sb, 1)

                    for k in range(12):
                        if k > 1:
                            split_unit(g0 + 1 + k // 2, k % 2)
                        if k == 2:
                            act.wait_ge(bias_in, 16)
                            act.activation(bh, bias, ACT.Copy).then_inc(bh_done, 1)
                        if k >= 4:
                            softmax(k - 4)
                        if k >= 5:
                            pt_copy(k - 5)
                    pt_copy(7)
                    for p in range(4):
                        act.wait_ge(o_mm, o_count(layer) + p + 1)
                        act.activation(oh[:, 2 * p:2 * p + 2, :],
                                       o_banks[p][:, :].rearrange("p (a b) -> p a b", a=2), ACT.Copy)\
                            .then_inc(oh_done, 1)
                    split(g0 + 7)
                else:
                    act.wait_ge(col_ready, n // 2 + 1)
                    for c in range(2):
                        for t in range(TT):
                            act.wait_ge(bank_ready, b0 + 2 * c + t + 1)
                            act.activation(yh[:, t, c * CH:(c + 1) * CH], acc[2 * c + t][:, :], ACT.Copy,
                                           scale=rcol[:, t:t + 1]).then_inc(yh_done, 1)
                g = first_group[f"mlp{layer}"]
                take_x(n + 1, {} if layer % 3 == 2 else {1: lambda: split(g)})

                g, b = first_group[f"mlp{layer}"], first_bank[f"mlp{layer}"]
                r0 = 2 * NCH * layer

                def hidden(par, b_at, r_at, down_at=None, first=False):
                    for i in range(2):
                        act.wait_ge(bank_ready, b_at + (i + 1))
                        if not first:
                            act.wait_ge(s_done, r_at + (i - 1))
                        act.activation(act_r[:, i, :], hb[i][:, :], ACT.Relu).then_inc(relu_done, 1)
                        if first and i == 0:
                            rms(n + 1)
                        act.wait_ge(s_done, r_at + (i + 1))
                        if down_at is not None:
                            act.wait_ge(down_done, down_at)
                        act.activation(hh[:, par, 2 * i:2 * i + 2, :],
                                       act_s[:, i, :].rearrange("p (a b) -> p a b", a=2), ACT.Copy)\
                            .then_inc(hh_done, 1)

                split(g + 1)
                hidden(0, b, r0, first=True)
                split(g + 2)
                hidden(1, b + 2, r0 + 2)
                split(g + 3)
                with act.Fori(0, (NCH - 2) // 2) as it:
                    for c in range(2):
                        split(g + 4 + 2 * c, it)
                        hidden(c, 4 * it + (b + 4 + 2 * c), 4 * it + (r0 + 4 + 2 * c),
                               2 * it + ((NCH - 1) * layer + 1 + c))
                        split(g + 5 + 2 * c, it)
                if layer == 2:
                    after_dve()
                    turn(act.activation(lb_in, carve(9216, 2, D), ACT.Exp))
                if g + 2 * NCH < n_groups:
                    if layer == 1:
                        act.wait_ge(band_loaded, 16)
                    split(g + 2 * NCH)
                if layer == 2:
                    after_dve()
                    turn(act.activation(lb_a, lb_a, ACT.Ln))
                take_x(n + 2)
            rms(2 * DEPTH)

        @block.vector
        def _(dve):
            ch = Chain(dve, dve_chain)

            def split_unit(g, u, it=None, n=2048):
                at = 2 * g + u + 1
                dve.wait_ge(hi_done, at if it is None else 8 * it + at)
                dve.tensor_tensor(wlo[:, g % 2, u, 0:n], raw[:, g % 2, u, 0:n],
                                  whi[:, g % 2, u, 0:n].bitcast(F32), ALU.subtract).then_inc(lo_done, 1)

            def split(g, it=None, n=2048):
                for u in range(2):
                    split_unit(g, u, it, n)

            def take_x(n, update, between={}):
                def lo(f):
                    dve.wait_ge(xh_done, 8 * n + f + 1)
                    ch.did(dve.scalar_tensor_tensor(out=xl[:, f, :], in0=xT[:, f, :],
                                                    scalar=gains[:, gain_col(n, f):gain_col(n, f) + 1],
                                                    in1=xh[:, f, :].bitcast(F32), op0=ALU.mult, op1=ALU.subtract),
                           xl_done)

                for k in range(4):
                    update(k)
                    if n < 2 * DEPTH and k:
                        lo(2 * k - 2)
                        lo(2 * k - 1)
                    if k in between:
                        between[k]()
                if n < 2 * DEPTH:
                    lo(6)
                    lo(7)

            def column(n):
                dve.wait_ge(col_mm, n // 2 + 1)
                ch.did(dve.tensor_copy(rcol[:, :], misc[1][:, 0:SEQ:P]), col_ready)
                ch.settle()

            dve.wait_ge(gains_T, 1)
            ch.did(dve.tensor_copy(gains[:, :], misc[1][:, 0:82]), gains_sb)
            ch.settle()

            def start(k):
                dve.wait_ge(xT_mm, k + 1)
                ch.did(dve.tensor_copy(xT[:, 2 * k:2 * k + 2, :], acc[k][:, :].rearrange("p (a b) -> p a b", a=2)),
                       x_ready)
                ch.settle()

            for k in range(4):
                start(k)
            take_x(0, lambda k: None, {2: lambda: split_unit(0, 0), 3: lambda: split_unit(0, 1)})
            dve.wait_ge(decay_loaded, 32)
            ch.did(dve.tensor_copy(mask64, masks_in[:, 0, :]))
            ch.did(dve.tensor_copy(masks[:, :, :], masks_in))
            ch.settle()

            turns = {"act": 0, "dve": 0}

            def turn(ins):
                ch.did(ins, gate_dve)
                turns["dve"] += 1

            def after_act():
                turns["act"] += 1
                dve.wait_ge(gate_act, turns["act"])

            for layer in range(DEPTH):
                n = mix_norm(layer)
                g0, b0 = first_group[f"in{layer}"], first_bank[f"in{layer}"]
                j = layer // 3
                split(g0 + 1)
                if layer % 3 != 1:
                    column(n)
                if layer % 3 == 0:
                    def gate_a(c, t):
                        cs = slice(c * CH, (c + 1) * CH)
                        z = v[:, t, cs]
                        s1, s2 = scratch[t]
                        after_act()
                        ch.settle()
                        ch.did(dve.scalar_tensor_tensor(out=s2, in0=z, scalar=0.0, in1=s1,
                                                        op0=ALU.min, op1=ALU.subtract))
                        ch.settle()
                        if layer == 0:
                            turn(dve.tensor_tensor(v[:, t, cs], s2, z, ALU.subtract))
                        else:
                            ch.did(dve.tensor_tensor(s2, s2, C1[:, cs], ALU.add))
                            ch.settle()
                            ch.did(dve.tensor_tensor(v[:, t, cs], s2, z, ALU.subtract))
                            turn(dve.tensor_tensor(s1, C0[:, cs], s2, ALU.subtract))
                            ch.settle()
                            ch.did(dve.tensor_tensor(s2, s2, C0[:, cs], ALU.max))

                    def gate_b(c, t):
                        if layer == 3:
                            s1, s2 = scratch[t]
                            after_act()
                            ch.settle()
                            turn(dve.tensor_tensor(s2, s2, s1, ALU.add))

                    def gate_c(c, t):
                        cs = slice(c * CH, (c + 1) * CH)
                        after_act()
                        ch.settle()
                        ch.did(dve.tensor_tensor(lfl[:, t, cs], scratch[t][1], lfh[:, t, cs].bitcast(F32),
                                                 ALU.subtract), lf_ready)

                    def silu_z(k, z):
                        dve.wait_ge(bank_ready, b0 + k + 1)
                        ch.did(dve.tensor_tensor(z, hb[k % 2][:, :].rearrange("p (a b) -> p a b", a=2),
                                                 rstd[:, :].rearrange("p (a b) -> p a b", a=1)
                                                 .to_broadcast([P, 2, SEQ]), ALU.mult),
                               bank_free, free_count(layer) + k - 3)

                    def silu_a(s, z):
                        s1, s2 = (w.rearrange("p (a b) -> p a b", a=2) for w in scratch[s])
                        after_act()
                        ch.settle()
                        turn(dve.scalar_tensor_tensor(out=s2, in0=z, scalar=0.0, in1=s1,
                                                      op0=ALU.min, op1=ALU.subtract))

                    def silu_b(s, z):
                        after_act()
                        ch.settle()
                        ch.did(dve.tensor_tensor(z, z, scratch[s][0].rearrange("p (a b) -> p a b", a=2), ALU.mult),
                               silu_done)

                    def q_bank(k):
                        return qT[:, 2 * (k - 4):2 * (k - 4) + 2, :]

                    for c in range(2):
                        gate_a(c, 0)
                        split_unit(g0 + 2 + c, 0)
                        if c:
                            silu_z(4, q_bank(4))
                            split_unit(g0 + 3, 1)
                        gate_a(c, 1)
                        if not c:
                            split_unit(g0 + 2, 1)
                        if c:
                            silu_z(5, q_bank(5))
                        gate_b(c, 0)
                        gate_b(c, 1)
                        gate_c(c, 0)
                        gate_c(c, 1)
                    silu_a(0, q_bank(4))
                    silu_a(1, q_bank(5))
                    split_unit(g0 + 4, 0)
                    silu_b(0, q_bank(4))
                    silu_b(1, q_bank(5))
                    silu_z(6, q_bank(6))
                    split_unit(g0 + 4, 1)
                    silu_z(7, q_bank(7))
                    silu_a(0, q_bank(6))
                    silu_a(1, q_bank(7))
                    silu_b(0, q_bank(6))
                    silu_b(1, q_bank(7))

                    def pq_step(i):
                        h, p = i // 4, i % 2
                        dve.wait_ge(ex_done, 32 * j + i + 1)
                        if i >= 2:
                            dve.wait_ge(g_mm, 40 * j + 5 * ((i - 2) // 4) + (i - 2) % 4 + 1)
                        ch.did(dve.tensor_tensor(
                            Pq[:, p, :].rearrange("p (t l x) -> p t l x", t=2, l=2),
                            Ex[:, p, :].rearrange("p (t l x) -> p t l x", t=2, l=2),
                            qT[:, h, :].rearrange("p (t l x) -> p t l x", t=2, l=1).to_broadcast([P, 2, 2, P]),
                            ALU.mult), pq_done)

                    def select(i):
                        h, c = divmod(i, 5)
                        gb = acc[2 + i % 2]
                        own = att[:, h, :].rearrange("p (a x) -> p a x", a=3)[:, 0:3:2, :]
                        dve.wait_ge(g_mm, 40 * j + i + 1)
                        levels = [2 * c, 2 * c + 1] if c < 3 else ([6] if c == 3 else [7])
                        for k, lev in enumerate(levels):
                            part = gb[:, k * 256:(k + 1) * 256].rearrange("p (a x) -> p a x", a=2)
                            ch.settle()
                            if lev == 0:
                                ins = dve.tensor_tensor(own, part, mask64.rearrange("p (a x) -> p a x", a=1)
                                                        .to_broadcast([P, 2, P]), ALU.mult)
                            else:
                                ins = dve.copy_predicated(own, masks[:, lev:lev + 1, :].to_broadcast([P, 2, P]), part)
                            last = k == len(levels) - 1 and c != 3
                            ch.did(ins, g_read if last else None)
                        if c == 3:
                            ch.did(dve.tensor_copy(att[:, h, P:2 * P], gb[:, 256:384]), g_read)

                    for k in range(8):
                        if 1 <= k <= 4:
                            c, t = divmod(k - 1, 2)
                            dve.wait_ge(bank_ready, b0 + 8 + k)
                            if c == 0:
                                dve.wait_ge(kT_sb, 4 * (j + 1))
                            ch.did(dve.tensor_scalar(v[:, t, c * CH:(c + 1) * CH], hb[t][:, :], rcol[:, t:t + 1],
                                                     None, ALU.mult), bank_free, free_count(layer) + 4 + k)
                        if k > 4:
                            z = hn[:, 2 * (k - 5):2 * (k - 5) + 2, :]
                            silu_z(7 + k, z)
                        for m in range(4):
                            pq_step(4 * k + m)
                            if k > 4 and m == 1:
                                silu_a(0, z)
                            if 5 * k - 2 + m >= 0:
                                select(5 * k - 2 + m)
                            if k > 4 and m == 2:
                                silu_b(0, z)
                            if m == 0:
                                split_unit(g0 + 5 + k // 2, k % 2)
                        select(5 * k + 2)
                    def o_norm(p):
                        dve.wait_ge(ors_done, 4 * j + p + 1)
                        ch.settle()
                        r = Ex[:, p % 2, :]
                        ch.did(dve.tensor_tensor(r, o_banks[p][:, :], r, ALU.mult))
                        ch.settle()
                        ch.did(dve.scalar_tensor_tensor(out=o_at[p].rearrange("p (a b) -> p a b", a=2),
                                                        in0=r.rearrange("p (a b) -> p a b", a=2),
                                                        scalar=gains[:, 80 + j:81 + j],
                                                        in1=hn[:, 2 * p:2 * p + 2, :],
                                                        op0=ALU.mult, op1=ALU.mult), on_done)

                    def o_lo(p):
                        dve.wait_ge(oh_done, o_count(layer) + p + 1)
                        ch.did(dve.tensor_tensor(ol[:, 2 * p:2 * p + 2, :],
                                                 o_at[p].rearrange("p (a b) -> p a b", a=2),
                                                 oh[:, 2 * p:2 * p + 2, :].bitcast(F32), ALU.subtract), ol_done)

                    select(38)
                    silu_z(15, hn[:, 6:8, :])
                    select(39)
                    silu_a(0, hn[:, 6:8, :])
                    o_norm(0)
                    silu_b(0, hn[:, 6:8, :])
                    o_norm(1)
                    o_lo(0)
                    o_lo(1)
                    o_norm(2)
                    o_norm(3)
                    o_lo(2)
                    o_lo(3)
                    split(first_group[f"out{layer}"] + 1)
                elif layer % 3 == 1:
                    dve.wait_ge(bias_row_mm, 1)
                    ch.did(dve.tensor_copy(bias_row, misc[1][0:HEADS, :]), bias_row_sb)
                    def row_max(h):
                        dve.wait_ge(s_mm, h + 1)
                        k = 2 * (h % 2)
                        if h >= 2:
                            dve.wait_ge(sexp, 2 * (h - 1))
                            ch.settle()
                        ch.did(dve.tensor_reduce(small[:, k:k + 1], acc[h % 2][:, 0:P], AX.X, ALU.max))
                        ch.did(dve.tensor_reduce(small[:, k + 1:k + 2], acc[h % 2][:, P:3 * P], AX.X, ALU.max))
                        ch.settle()
                        ch.did(dve.tensor_scalar(small[:, 4 + k:6 + k], small[:, k:k + 2], -1.0, None, ALU.mult), smax)

                    def normalise(h):
                        k = 2 * (h % 2)
                        dve.wait_ge(sexp, 2 * (h + 1))
                        ch.settle()
                        ch.did(dve.reciprocal(small[:, 12 + k:14 + k], small[:, 8 + k:10 + k]))
                        ch.settle()
                        for t, cs in ((0, slice(0, P)), (1, slice(P, 3 * P))):
                            ch.did(dve.tensor_scalar(probs[:, h % 2, cs], probs[:, h % 2, cs],
                                                     small[:, 12 + k + t:13 + k + t], None, ALU.mult), sscaled)

                    column(n)

                    def empty(k):
                        dve.wait_ge(bank_ready, b0 + k + 1)
                        c, i = divmod(k, 2)
                        h = 4 * (c // 2) + 2 * i
                        r = rstd[:, :].rearrange("p (a b) -> p a b", a=1).to_broadcast([P, 2, SEQ])
                        z = hb[i][:, :].rearrange("p (a b) -> p a b", a=2)
                        if c >= 4:
                            ins = dve.tensor_scalar(v[:, i, (c - 4) * CH:(c - 3) * CH], hb[i][:, :],
                                                    rcol[:, i:i + 1], None, ALU.mult)
                        elif c % 2 == 0:
                            ins = dve.scalar_tensor_tensor(out=qT[:, h:h + 2, :], in0=z, scalar=float(P) ** -0.5,
                                                           in1=r, op0=ALU.mult, op1=ALU.mult)
                        else:
                            ins = dve.tensor_tensor(kT[:, h:h + 2, :], z, r, ALU.mult)
                        ch.did(ins, bank_free, free_count(layer) + k + 1)

                    for k in range(12):
                        if k:
                            empty(k - 1)
                        if k > 1:
                            split_unit(g0 + 1 + k // 2, k % 2)
                        if k == 2:
                            dve.wait_ge(bh_done, 1)
                            ch.did(dve.tensor_tensor(bl, bias, bh.bitcast(F32), ALU.subtract), bl_done)
                        if k >= 4:
                            row_max(k - 4)
                            normalise(k - 4)
                    empty(11)
                    for p in range(4):
                        dve.wait_ge(oh_done, o_count(layer) + p + 1)
                        ch.did(dve.tensor_tensor(ol[:, 2 * p:2 * p + 2, :],
                                                 o_banks[p][:, :].rearrange("p (a b) -> p a b", a=2),
                                                 oh[:, 2 * p:2 * p + 2, :].bitcast(F32), ALU.subtract), ol_done)
                    split(g0 + 7)
                else:
                    for c in range(2):
                        for t in range(TT):
                            cs = slice(c * CH, (c + 1) * CH)
                            dve.wait_ge(yh_done, 2 * c + t + 1)
                            ch.did(dve.scalar_tensor_tensor(out=yl[:, t, cs], in0=acc[2 * c + t][:, :],
                                                            scalar=rcol[:, t:t + 1], in1=yh[:, t, cs].bitcast(F32),
                                                            op0=ALU.mult, op1=ALU.subtract), yl_done)
                    dve.wait_ge(inv_in, 16)

                bo = first_bank.get(f"out{layer}")

                def mixed(k):
                    if layer % 3 == 2:
                        dve.wait_ge(pool_mm, k + 1)
                        z = scaled[:, k % 2, :].rearrange("p (a b) -> p a b", a=2)
                        ch.did(dve.tensor_tensor(z, hb[k % 2][:, :].rearrange("p (a b) -> p a b", a=2),
                                                 inv[:, k:k + 1, :].to_broadcast([P, 2, SEQ]), ALU.mult))
                        ch.settle()
                    else:
                        dve.wait_ge(bank_ready, bo + k + 1)
                    pair = slice(2 * k, 2 * k + 2)
                    if layer % 3 == 2:
                        for i in range(2):
                            f = 2 * k + i
                            ins = dve.scalar_tensor_tensor(out=xT[:, f, :], in0=z[:, i, :],
                                                           scalar=gains[:, 72 + f:73 + f], in1=xT[:, f, :],
                                                           op0=ALU.mult, op1=ALU.add)
                            ch.did(ins, x_ready if i else None)
                    else:
                        ch.did(dve.tensor_tensor(xT[:, pair, :], hb[k % 2][:, :].rearrange("p (a b) -> p a b", a=2),
                                                 xT[:, pair, :], ALU.add), x_ready)
                    ch.settle()

                g = first_group[f"mlp{layer}"]
                take_x(n + 1, mixed, {} if layer % 3 == 2 else {1: lambda: split(g)})

                g = first_group[f"mlp{layer}"]
                r0 = 2 * NCH * layer

                def hidden(par, r_at, first=False):
                    for i in range(2):
                        dve.wait_ge(relu_done, r_at + (i + 1))
                        if not first:
                            dve.wait_ge(hh_done, r_at + (i - 1))
                            dve.wait_ge(hl_done, r_at + (i - 1))
                        dve.tensor_tensor(act_s[:, i, :].rearrange("p (a b) -> p a b", a=2),
                                          act_r[:, i, :].rearrange("p (a b) -> p a b", a=2),
                                          rstd[:, :].rearrange("p (a b) -> p a b", a=1).to_broadcast([P, 2, SEQ]),
                                          ALU.mult).then_inc(scaled_done, 1)
                        dve.wait_ge(scaled_done, r_at + (i + 1))
                        dve.tensor_tensor(act_s[:, i, :], act_s[:, i, :], act_s[:, i, :], ALU.mult).then_inc(s_done, 1)
                        dve.wait_ge(hh_done, r_at + (i + 1))
                        dve.tensor_tensor(hl[:, par, 2 * i:2 * i + 2, :],
                                          act_s[:, i, :].rearrange("p (a b) -> p a b", a=2),
                                          hh[:, par, 2 * i:2 * i + 2, :].bitcast(F32), ALU.subtract).then_inc(hl_done, 1)

                split(g + 1)
                dve.wait_ge(rstd_ready, n + 2)
                hidden(0, r0, first=True)
                split(g + 2)
                hidden(1, r0 + 2)
                split(g + 3)
                if layer == 2:
                    dve.wait_ge(lb_loaded, 16)
                    ch.settle()
                    ch.did(dve.tensor_tensor(lb_a, lb_in[:, 0, :], lb_in[:, 1, :], ALU.max))
                    ch.settle()
                    ch.did(dve.tensor_tensor(C0, lb_in[:, 1, :], lb_a, ALU.subtract))
                    turn(dve.tensor_tensor(C1, lb_in[:, 0, :], lb_a, ALU.subtract))
                with dve.Fori(0, (NCH - 2) // 2) as it:
                    for c in range(2):
                        split(g + 4 + 2 * c, it)
                        hidden(c, 4 * it + (r0 + 4 + 2 * c))
                        split(g + 5 + 2 * c, it)
                if layer == 2:
                    after_act()
                    turn(dve.tensor_tensor(lb_a, lb_in[:, 0, :], lb_in[:, 1, :], ALU.add))
                if g + 2 * NCH < n_groups:
                    split(g + 2 * NCH)
                if layer == 2:
                    after_act()
                    ch.settle()
                    ch.did(dve.tensor_tensor(C0, C0, lb_a, ALU.subtract))
                    turn(dve.tensor_tensor(C1, C1, lb_a, ALU.subtract))

                def mlp_out(k):
                    dve.wait_ge(acc_ready, 4 * layer + k + 1)
                    ch.did(dve.tensor_tensor(xT[:, 2 * k:2 * k + 2, :], acc[k][:, :].rearrange("p (a b) -> p a b", a=2),
                                             xT[:, 2 * k:2 * k + 2, :], ALU.add), x_ready)
                    ch.settle()

                take_x(n + 2, mlp_out)

            dve.wait_ge(rstd_ready, 2 * DEPTH + 1)
            for f in range(KT):
                col = gain_col(2 * DEPTH, f)
                ch.did(dve.scalar_tensor_tensor(out=hn[:, f, :], in0=xT[:, f, :], scalar=gains[:, col:col + 1],
                                                in1=rstd[:, :], op0=ALU.mult, op1=ALU.mult), hn_done)

            for t in range(TT):
                for c in range(2):
                    dve.wait_ge(out_mm, 2 * t + c + 1)
                    ch.did(dve.tensor_copy(x_tok[:, t, c * CH:(c + 1) * CH], acc[2 * t + c][:, :]), out_sb)

        @block.gpsimd
        def _(pool):
            ch = Chain(pool, pool_chain)
            ch.did(pool.memset(ident[:, :], 0.0))
            ch.settle()
            ch.did(pool.memset(flip_in, 0.0))
            ch.settle()
            ch.did(pool.affine_select(out=ident[:, :], in_=ident[:, :], compare_op=ALU.not_equal, fill=1.0, base=0,
                                      pattern=[[-1, P]], channel_multiplier=1), pool_const)
            ch.settle()
            ch.did(pool.memset(ones[:, :], 1.0), pool_const)
            ch.settle()
            ch.did(pool.memset(eps_col[:, :], EPS), pool_const)
            ch.settle()
            ch.did(pool.memset(tab[BUCKETS:BUCKETS + 1, :], MASKED), pool_const)
            ch.settle()
            ch.did(pool.affine_select(out=flip_in, in_=flip_in, compare_op=ALU.not_equal, fill=1.0, base=1 - P,
                                      pattern=[[1, P]], channel_multiplier=1))
            ch.settle()
            ch.did(pool.tensor_copy(flip[:, :], flip_in), pool_const)

            def sum_squares(n):
                pool.wait_ge(sq_ready, 2 * n + 1)
                if n:
                    pool.wait_ge(ms_mm, n)
                ch.settle()
                ch.did(pool.tensor_tensor(squares[:, :, :], hn[:, 0:2, :], hn[:, 2:4, :], ALU.add))
                pool.wait_ge(sq_ready, 2 * n + 2)
                ch.settle()
                ch.did(pool.tensor_tensor(hn[:, 4:6, :], hn[:, 4:6, :], hn[:, 6:8, :], ALU.add))
                ch.settle()
                ch.did(pool.tensor_tensor(squares[:, :, :], squares[:, :, :], hn[:, 4:6, :], ALU.add), sum_ready)

            sum_squares(0)
            for layer in range(DEPTH):
                n = mix_norm(layer)
                j = layer // 3
                if layer % 3 == 0:
                    for i in range(32):
                        h, p = i // 4, i % 2
                        pool.wait_ge(ex_done, 32 * j + i + 1)
                        if i == 0:
                            pool.wait_ge(kT_sb, 4 * (j + 1))
                        if i >= 2:
                            pool.wait_ge(g_mm, 40 * j + 5 * ((i - 2) // 4) + (i - 2) % 4 + 1)
                        pool.tensor_tensor(
                            Pk[:, p, :].rearrange("p (t l x) -> p t l x", t=2, l=2),
                            Ex[:, p, :].rearrange("p (t l x) -> p t l x", t=2, l=2),
                            kT[:, h, :].rearrange("p (t l x) -> p t l x", t=2, l=1).to_broadcast([P, 2, 2, P]),
                            ALU.mult).then_inc(pk_done, 1)
                elif layer % 3 == 1:
                    pool.wait_ge(bias_row_sb, 1)
                    pool.dma_start(bias_dram, bias_row).then_inc(bias_out, 16)
                sum_squares(n + 1)
                if layer < DEPTH - 1:
                    sum_squares(n + 2)


_INS = ['x', 'norm_mix', 'norm_mlp', 'norm_final', 'a_w_in', 'a_lower_bound', 'a_head_norm', 'a_w_out', 'b_w_qkv',
        'b_w_out', 'rel_bias', 'c_w_group', 'c_scale', 'mlp_w1', 'mlp_w2']
_OUTS = [((1, SEQ, D), 'float32')]


def kernel(**inputs):
    import concourse.bacc as _bacc
    from concourse.bass_utils import run_bass_kernel_spmd as _run

    nc = _bacc.Bacc("TRN2", target_bir_lowering=False, num_devices=1)
    arrays, args = {}, []
    given = {name: np.ascontiguousarray(inputs[name]) for name in _INS}
    given |= {'decay': decay_sums(), 'mask': level_masks(), 'bucket': bucket_rows(), 'inv': inverse_counts(),
              'band': pool_band()}
    for name, a in given.items():
        arrays[f"in_{name}_dram"] = a
        args.append(nc.dram_tensor(f"in_{name}_dram", a.shape, mybir.dt.from_np(a.dtype), kind="ExternalInput").ap())
    for i, (shape, dtype) in enumerate(_OUTS):
        dt = mybir.dt.from_np(np.dtype(dtype))
        args.append(nc.dram_tensor(f"out_{i}_dram", shape, dt, kind="ExternalOutput").ap())
    build_decoder(nc, *args)
    r = _run(nc, [arrays], core_ids=[0])
    return r.results[0]["out_0_dram"]
```
